# Optimizing a Trainium2 kernel written in Bass

```python
import jax, jax.numpy as jnp
from jax import lax
import numpy as np

D_MODEL = 1024
BATCH = 1
SEQ = 512
DEPTH = 2
DEC_BATCH = 8
DEC_SEQ = 16
PAST_LEN = 1024

CHUNK = 64
N_MIXERS = 2
N_ATTN = (DEPTH + 1) // 2
N_GMLP = DEPTH // 2
N_HEADS = 8
HEAD_DIM = D_MODEL // N_HEADS
N_KV_HEADS = 2
ROPE_FRAC_DIV = 4
ROPE_THETA = 500000.0
N_IDX_HEADS = 8
IDX_DIM = 64
TOPK_MAX = 256
Q_BLOCK = 128
O_Q = N_HEADS * HEAD_DIM
O_K = O_Q + N_KV_HEADS * HEAD_DIM
O_V = O_K + N_KV_HEADS * HEAD_DIM
O_QI = O_V + N_IDX_HEADS * IDX_DIM
O_KI = O_QI + IDX_DIM
ATTN_PROJ = O_KI + N_IDX_HEADS
D_GM = D_MODEL
GM_GROUPS = 8
GM_CHUNK = 128
D_FF = 2816
CONV_W = 3
PLE_DIM = 256
EPS = 1e-6
NEG_INF = -1e30

kernel_name = 'hybrid_dsa_gmlp_streaming_step'

def rms_norm(x, g):
    xf = x.astype(jnp.float32)
    y = xf * lax.rsqrt(jnp.mean(xf * xf, axis=-1, keepdims=True) + EPS)
    return (y * g.astype(jnp.float32)).astype(x.dtype)

def partial_rope(x, pos):
    d = x.shape[-1]
    r = d // ROPE_FRAC_DIV
    half = r // 2
    inv = ROPE_THETA ** (-jnp.arange(half, dtype=jnp.float32) * (2.0 / r))
    ang = pos.astype(jnp.float32)[:, None] * inv[None, :]
    cos = jnp.cos(ang)[None, :, None, :]
    sin = jnp.sin(ang)[None, :, None, :]
    xf = x.astype(jnp.float32)
    x1 = xf[..., :half]
    x2 = xf[..., half:r]
    out = jnp.concatenate([x1 * cos - x2 * sin, x2 * cos + x1 * sin, xf[..., r:]], axis=-1)
    return out.astype(x.dtype)

def attn_project(h, w_in, q_g, k_g, pos):
    B, T, _ = h.shape
    z = h @ w_in
    q = z[..., :O_Q].reshape(B, T, N_HEADS, HEAD_DIM)
    k = z[..., O_Q:O_K].reshape(B, T, N_KV_HEADS, HEAD_DIM)
    v = z[..., O_K:O_V].reshape(B, T, N_KV_HEADS, HEAD_DIM)
    qi = z[..., O_V:O_QI].reshape(B, T, N_IDX_HEADS, IDX_DIM)
    ki = z[..., O_QI:O_KI].reshape(B, T, 1, IDX_DIM)
    wi = z[..., O_KI:]
    q = partial_rope(rms_norm(q, q_g), pos)
    k = partial_rope(rms_norm(k, k_g), pos)
    qi = partial_rope(qi, pos)
    ki = partial_rope(ki, pos)[:, :, 0]
    return q, k, v, qi, ki, wi

def sparse_attend(q, qi, wi, q_pos, k, v, ki, k_sel):
    B, Tq = q.shape[0], q.shape[1]
    L = k.shape[1]
    s = jnp.einsum('bqhd,bkd->bqhk', qi.astype(jnp.float32), ki.astype(jnp.float32)) * (IDX_DIM ** -0.5)
    score = jnp.einsum('bqhk,bqh->bqk', jax.nn.relu(s), wi.astype(jnp.float32) * (N_IDX_HEADS ** -0.5))
    limit = (q_pos // CHUNK + 1) * CHUNK
    admissible = jnp.arange(L, dtype=jnp.int32)[None, :] < limit[:, None]
    score = jnp.where(admissible[None], score, NEG_INF)
    _, idx = lax.top_k(score, k_sel)
    valid = idx < limit[None, :, None]
    kg = jax.vmap(lambda kb, ib: kb[ib])(k, idx)
    vg = jax.vmap(lambda vb, ib: vb[ib])(v, idx)
    qg = q.reshape(B, Tq, N_KV_HEADS, N_HEADS // N_KV_HEADS, HEAD_DIM)
    logits = jnp.einsum('bqgrd,bqkgd->bqgrk', qg.astype(jnp.float32), kg.astype(jnp.float32)) * (HEAD_DIM ** -0.5)
    logits = jnp.where(valid[:, :, None, None, :], logits, NEG_INF)
    p = jax.nn.softmax(logits, axis=-1).astype(v.dtype)
    o = jnp.einsum('bqgrk,bqkgd->bqgrd', p, vg)
    return o.reshape(B, Tq, N_HEADS * HEAD_DIM)

def attn_mixer_prompt(h, w_in, q_g, k_g, w_out):
    B, T, _ = h.shape
    pos = jnp.arange(T, dtype=jnp.int32)
    q, k, v, qi, ki, wi = attn_project(h, w_in, q_g, k_g, pos)
    k_sel = min(TOPK_MAX, T // 4)
    nb = T // Q_BLOCK

    def to_blocks(a):
        return jnp.moveaxis(a.reshape((B, nb, Q_BLOCK) + a.shape[2:]), 1, 0)

    def one_block(args):
        qb, qib, wib, pb = args
        return sparse_attend(qb, qib, wib, pb, k, v, ki, k_sel)

    o = lax.map(one_block, (to_blocks(q), to_blocks(qi), to_blocks(wi), pos.reshape(nb, Q_BLOCK)))
    o = jnp.moveaxis(o, 0, 1).reshape(B, T, N_HEADS * HEAD_DIM)
    return o @ w_out, k, v, ki

def attn_mixer_sample(h, ck, cv, cki, w_in, q_g, k_g, w_out):
    B, T, _ = h.shape
    P = ck.shape[1]
    pos = P + jnp.arange(T, dtype=jnp.int32)
    q, k, v, qi, ki, wi = attn_project(h, w_in, q_g, k_g, pos)
    k_all = jnp.concatenate([ck, k], axis=1)
    v_all = jnp.concatenate([cv, v], axis=1)
    ki_all = jnp.concatenate([cki, ki], axis=1)
    k_sel = min(TOPK_MAX, (P + T) // 4)
    o = sparse_attend(q, qi, wi, pos, k_all, v_all, ki_all, k_sel)
    return o @ w_out, k, v, ki

def gmlp_mixer(h, w_in, v_g, w_s, b_s, w_out):
    B, T, _ = h.shape
    z = jax.nn.gelu(h @ w_in)
    u = z[..., :D_GM]
    v = rms_norm(z[..., D_GM:], v_g)
    Tc = min(T, GM_CHUNK)
    nc = T // Tc
    mask = jnp.tril(jnp.ones((Tc, Tc), dtype=w_s.dtype))
    ws = w_s[:, :Tc, :Tc] * mask
    vb = v.reshape(B, nc, Tc, GM_GROUPS, D_GM // GM_GROUPS)
    mixed = jnp.einsum('gts,bnsgd->bntgd', ws, vb) + b_s[:, :Tc].T[None, None, :, :, None]
    s = u * mixed.reshape(B, T, D_GM)
    return s @ w_out, v

def conv_ffn(h, past, w_up, conv_w, conv_b, w_down):
    T = h.shape[1]
    a = h @ w_up
    full = jnp.concatenate([past, a], axis=1)
    c = conv_b
    for j in range(CONV_W):
        c = c + conv_w[j] * full[:, j:j + T]
    g = c[..., :D_FF]
    up = c[..., D_FF:]
    return (jax.nn.silu(g) * up) @ w_down, full[:, T:]

def ple_add(h, p, g, w_gate, w_proj):
    return h + jax.nn.sigmoid(rms_norm(h, g) @ w_gate) * (p @ w_proj)

def setup_inputs(seed: int = 0) -> dict:
    key = jax.random.key(seed)
    ks = jax.random.split(key, 32)
    f32 = jnp.float32

    def nrm(k, shape, scale):
        return jax.random.normal(k, shape, f32) * scale

    def gain(k, shape):
        return 1.0 + 0.05 * jax.random.normal(k, shape, f32)

    return {
        'x_prompt': nrm(ks[0], (BATCH, SEQ, D_MODEL), 1.0),
        'x_sample': nrm(ks[1], (DEC_BATCH, DEC_SEQ, D_MODEL), 1.0),
        'cache_k': nrm(ks[2], (N_ATTN, DEC_BATCH, PAST_LEN, N_KV_HEADS, HEAD_DIM), 1.0),
        'cache_v': nrm(ks[3], (N_ATTN, DEC_BATCH, PAST_LEN, N_KV_HEADS, HEAD_DIM), 1.0),
        'cache_kidx': nrm(ks[4], (N_ATTN, DEC_BATCH, PAST_LEN, IDX_DIM), 1.0),
        'state_ffn_conv': nrm(ks[5], (DEPTH, DEC_BATCH, CONV_W - 1, 2 * D_FF), 1.0),
        'p_prompt': nrm(ks[6], (DEPTH, BATCH, SEQ, PLE_DIM), 1.0),
        'p_sample': nrm(ks[7], (DEPTH, DEC_BATCH, DEC_SEQ, PLE_DIM), 1.0),
        'norm_mix': gain(ks[8], (DEPTH, D_MODEL)),
        'attn_w_in': nrm(ks[9], (N_ATTN, D_MODEL, ATTN_PROJ), D_MODEL ** -0.5),
        'attn_q_norm': gain(ks[10], (N_ATTN, HEAD_DIM)),
        'attn_k_norm': gain(ks[11], (N_ATTN, HEAD_DIM)),
        'attn_w_out': nrm(ks[12], (N_ATTN, N_HEADS * HEAD_DIM, D_MODEL), (N_HEADS * HEAD_DIM) ** -0.5),
        'gmlp_w_in': nrm(ks[13], (N_GMLP, D_MODEL, 2 * D_GM), D_MODEL ** -0.5),
        'gmlp_v_norm': gain(ks[14], (N_GMLP, D_GM)),
        'gmlp_w_spatial': nrm(ks[15], (N_GMLP, GM_GROUPS, GM_CHUNK, GM_CHUNK), GM_CHUNK ** -0.5),
        'gmlp_b_spatial': gain(ks[16], (N_GMLP, GM_GROUPS, GM_CHUNK)),
        'gmlp_w_out': nrm(ks[17], (N_GMLP, D_GM, D_MODEL), D_GM ** -0.5),
        'norm_ffn': gain(ks[18], (DEPTH, D_MODEL)),
        'ffn_w_up': nrm(ks[19], (DEPTH, D_MODEL, 2 * D_FF), D_MODEL ** -0.5),
        'ffn_conv_w': nrm(ks[20], (DEPTH, CONV_W, 2 * D_FF), CONV_W ** -0.5),
        'ffn_conv_b': nrm(ks[21], (DEPTH, 2 * D_FF), 0.01),
        'ffn_w_down': nrm(ks[22], (DEPTH, D_FF, D_MODEL), D_FF ** -0.5),
        'norm_ple': gain(ks[23], (DEPTH, D_MODEL)),
        'ple_w_gate': nrm(ks[24], (DEPTH, D_MODEL, D_MODEL), D_MODEL ** -0.5),
        'ple_w_proj': nrm(ks[25], (DEPTH, PLE_DIM, D_MODEL), PLE_DIM ** -0.5),
    }

def reference(x_prompt, x_sample, cache_k, cache_v, cache_kidx, state_ffn_conv, p_prompt, p_sample,
              norm_mix, attn_w_in, attn_q_norm, attn_k_norm, attn_w_out,
              gmlp_w_in, gmlp_v_norm, gmlp_w_spatial, gmlp_b_spatial, gmlp_w_out,
              norm_ffn, ffn_w_up, ffn_conv_w, ffn_conv_b, ffn_w_down,
              norm_ple, ple_w_gate, ple_w_proj):
    yp = x_prompt
    ys = x_sample
    kp_l, vp_l, kip_l, ks_l, vs_l, kis_l, gv_l, cp_l, cs_l = [], [], [], [], [], [], [], [], []
    for i in range(DEPTH):
        j = i // N_MIXERS
        hp = rms_norm(yp, norm_mix[i])
        hs = rms_norm(ys, norm_mix[i])
        if i % N_MIXERS == 0:
            op, kp, vp, kip = attn_mixer_prompt(hp, attn_w_in[j], attn_q_norm[j], attn_k_norm[j], attn_w_out[j])
            os_, ks_, vs_, kis = attn_mixer_sample(hs, cache_k[j], cache_v[j], cache_kidx[j],
                                                   attn_w_in[j], attn_q_norm[j], attn_k_norm[j], attn_w_out[j])
            kp_l.append(kp); vp_l.append(vp); kip_l.append(kip)
            ks_l.append(ks_); vs_l.append(vs_); kis_l.append(kis)
        else:
            op, _ = gmlp_mixer(hp, gmlp_w_in[j], gmlp_v_norm[j], gmlp_w_spatial[j], gmlp_b_spatial[j], gmlp_w_out[j])
            os_, gv = gmlp_mixer(hs, gmlp_w_in[j], gmlp_v_norm[j], gmlp_w_spatial[j], gmlp_b_spatial[j], gmlp_w_out[j])
            gv_l.append(gv)
        yp = yp + op
        ys = ys + os_
        zeros_past = jnp.zeros((yp.shape[0], CONV_W - 1, 2 * D_FF), dtype=yp.dtype)
        fp, cp = conv_ffn(rms_norm(yp, norm_ffn[i]), zeros_past, ffn_w_up[i], ffn_conv_w[i], ffn_conv_b[i], ffn_w_down[i])
        fs, cs = conv_ffn(rms_norm(ys, norm_ffn[i]), state_ffn_conv[i], ffn_w_up[i], ffn_conv_w[i], ffn_conv_b[i], ffn_w_down[i])
        cp_l.append(cp); cs_l.append(cs)
        yp = ple_add(yp + fp, p_prompt[i], norm_ple[i], ple_w_gate[i], ple_w_proj[i])
        ys = ple_add(ys + fs, p_sample[i], norm_ple[i], ple_w_gate[i], ple_w_proj[i])
    new_k_prompt = jnp.stack(kp_l, 0)
    new_v_prompt = jnp.stack(vp_l, 0)
    new_kidx_prompt = jnp.stack(kip_l, 0)
    new_k_sample = jnp.stack(ks_l, 0)
    new_v_sample = jnp.stack(vs_l, 0)
    new_kidx_sample = jnp.stack(kis_l, 0)
    new_gmlp_v_sample = jnp.stack(gv_l, 0)
    new_conv_prompt = jnp.stack(cp_l, 0)
    new_conv_sample = jnp.stack(cs_l, 0)
    return (yp, ys, new_k_prompt, new_v_prompt, new_kidx_prompt, new_k_sample, new_v_sample,
            new_kidx_sample, new_gmlp_v_sample, new_conv_prompt, new_conv_sample)


_drawn_inputs = setup_inputs


def setup_inputs(seed=0):
    import zlib

    import numpy as np

    out = dict(_drawn_inputs(seed))
    spreads = {}
    factors = {'attn_q_norm': 6.177, 'ffn_conv_b': 6.374, 'norm_ple': 5.291, 'gmlp_b_spatial': 2.678}
    for name, (base, spread) in spreads.items():
        noise = np.random.default_rng([zlib.crc32(name.encode()), seed]).standard_normal(out[name].shape)
        drawn = base * np.exp(spread * noise) if base else spread * noise
        out[name] = __import__('jax').numpy.asarray(drawn.astype(out[name].dtype))
    for name, factor in factors.items():
        out[name] = (out[name] * factor).astype(out[name].dtype)
    return out
```

```python
from contextlib import ExitStack

import concourse.bass as bass
from concourse import mybir

F32, F32R, BF16 = mybir.dt.float32, mybir.dt.float32r, mybir.dt.bfloat16
ACT = mybir.ActivationFunctionType
ALU = mybir.AluOpType
AX = mybir.AxisListType.X

P = 128
D = 1024
KC = D // P
TP, NB, TQ = 512, 8, 16
TS = NB * TQ
T = TP + TS
TT = T // P
PAST = 1024
KEYS = PAST + TQ
H, G, R = 8, 2, 4
HI = 8
DI = 64
FF = 2816
FC = FF // P
PARTS = (8, 8, 6)
PC = 2
WU = 256
CONV_ROOM = 7424
EPS = 1e-6
SCALE = float(P) ** -0.5
NEG = -1e30
TAKEN = -3e38
TOPK_P, TOPK_S = 128, 256
ZQ, ZK, ZV, ZQI, ZKI, ZW, ZEND = 0, 1024, 1280, 1536, 2048, 2112, 2120
PADW = 2 + TP + NB * (2 + TQ) + 16
CW = TP + NB * (2 + TQ)


def counts(keys):
    return {k: n + 1 for n, k in enumerate(keys)}


def phases():
    out = [("qkv", [KC] * 9), ("attn_out", [KC] * 4)]
    for l in range(2):
        if l:
            out += [("gmlp_v", [KC] * 4), ("gmlp_u", [KC] * 4), ("gmlp_out", [KC] * 4)]
        for q, n in enumerate(PARTS):
            out += [(f"up{l}{q}", [KC] * n), (f"down{l}{q}", [n] * 4)]
        out.append((f"ple{l}", [PC, KC] * 4))
    return out


PH = phases()
UNITS = [(name, i, k) for name, ks in PH for i, k in enumerate(ks)]
BASE = {}
for _n, (_name, _i, _k) in enumerate(UNITS):
    BASE.setdefault(_name, _n)
WIDTH = [WU if (name, i) != ("qkv", 8) else ZEND - 8 * WU for name, i, k in UNITS]
OFFSET = [0]
for _k, _w in zip(UNITS, WIDTH):
    OFFSET.append(OFFSET[-1] + P * _k[2] * _w)

OPERANDS = ["mix0", "attn", "ffn0", "ple0", "mix1", "gate", "ffn1", "ple1"]
NORMS = ["mix0", "ffn0", "ple0", "mix1", "ffn1", "ple1"]


def bass_hybrid_step(nc, weights, xT_in, pT_in, gains_in, qkgain_in, rope_in, ident_in, onehot_in, qeq_in,
                     keyT_in, val_in, kidxT_in, pastT_in, convw_in, vgain_in, spat_in, spat_s_in, sbias_in,
                     yT_out, k_out, v_out, ki_out, gv_out, conv_out):
    with ExitStack() as ctx:
        def sb(name, shape, dt=F32, stack=ctx):
            return stack.enter_context(nc.sbuf_tensor(name, shape, dt))

        def sem(name):
            return ctx.enter_context(nc.semaphore(name))

        xT = sb("xT", [P, KC, T])
        w_raw = [sb(f"w_raw{i}", [P, KC * WU]) for i in range(2)]
        square = sb("square", [P, 2, T])
        square_sum = sb("square_sum", [P, T])
        rms = sb("rms", [P, T])
        inv_rms = sb("inv_rms", [P, T])
        ident = sb("ident", [P, P])
        ident_b = sb("ident_b", [P, P], BF16)
        ones = sb("ones", [P, P])
        eps = sb("eps", [P, 1])
        gains = sb("gains", [P, 6, KC])
        convw = sb("convw", [P, 2, 2 * FC, 4])
        pastT = sb("pastT", [P, 2 * FC, 2 * NB])
        tails = sb("tails", [P, 2 * FC, 2 * (NB + 1)])
        rcol = sb("rcol", [P, 8, TT])
        small = sb("small", [P, 64])

        at = ExitStack()
        qT = sb("qT", [P, H, T], F32, at)
        kT = sb("kT", [P, G, T], F32, at)
        vtok = sb("vtok", [P, TT, G * P], F32, at)
        qiT = sb("qiT", [P, HI // 2, TP], F32, at)
        q_smp = sb("q_smp", [P, NB, H * TQ], F32, at)
        qi_blk = sb("qi_blk", [P, NB, P], F32, at)
        kiT = sb("kiT", [P, T], F32, at)
        wi = sb("wi", [P, TT, HI], F32, at)
        pj = ExitStack()
        w_hi_0 = [sb(f"w_hi_0{i}", [P, KC * WU], F32R, pj) for i in range(2)]
        w_lo_0 = [sb(f"w_lo_0{i}", [P, KC * WU], F32R, pj) for i in range(2)]
        a_hi_0 = sb("a_hi_0", [P, KC, T], F32R, pj)
        a_lo_0 = sb("a_lo_0", [P, KC, T], F32R, pj)
        z = [sb(f"z{i}", [P, TT, WU], F32, pj) for i in range(2)]
        zs = sb("zs", [P, TT, WU], F32, pj)
        rope = sb("rope", [P, TT, 48], F32, pj)
        qkgain = sb("qkgain", [P, 2, P], F32, pj)
        hstat = sb("hstat", [P, 3, TT * 2], F32, pj)
        pj.close()
        ad = ExitStack()
        key_b = [sb(f"key_b{i}", [P, G, KEYS], F32, ad) for i in range(2)]
        val_b = [sb(f"val_b{i}", [P, 9, G * P], F32, ad) for i in range(2)]
        kidx_b = [key_b[0][:, i, :] for i in range(2)]
        score_s = sb("score_s", [P, KEYS], F32, ad)
        score_p = [None] + [sb(f"score_p{j}", [P, (j + 1) * P], F32, ad) for j in range(1, 4)]
        bias_s = sb("bias_s", [P, KEYS], BF16, ad)
        bias_p = [sb(f"bias_p{j}", [P, (j + 1) * P], BF16, ad) for j in range(4)]
        onehot = sb("onehot", [P, NB * P], BF16, ad)
        probs = [sb(f"probs{i}", [P, KEYS], F32, ad) for i in range(2)]
        probsT = [sb(f"probsT{i}", [P, 9, P], F32, ad) for i in range(2)]
        qeq = sb("qeq", [P, TQ], F32, ad)
        w_rows = sb("w_rows", [P, P], F32, ad)
        w_sel = sb("w_sel", [P, NB * (P + TQ)], F32, ad)
        best = sb("best", [P, 4, 8], F32, ad)
        stat = sb("stat", [P, 4, 40], F32, ad)
        ad.close()
        at.close()
        g_hi = sb("g_hi", [P, 8, T], F32R)
        g_lo = sb("g_lo", [P, 8, T], F32R)
        spat = [sb(f"spat{i}", [P, 2, P]) for i in range(2)]
        sbias = [sb(f"sbias{i}", [P, P]) for i in range(2)]
        sb("spare", [P, 600])
        a_hi = sb("a_hi", [P, KC, T], F32R)
        a_lo = sb("a_lo", [P, KC, T], F32R)
        w_hi_1 = sb("w_hi_1", [P, KC * WU], F32R)
        w_lo_1 = sb("w_lo_1", [P, KC * WU], F32R)
        with ExitStack() as ff:
            conv_in = [[sb(f"conv_in{i}{j}", [P, PADW], F32, ff) for j in range(2)] for i in range(2)]
            conv = [[sb(f"conv{i}{j}", [P, CW], F32, ff) for j in range(2)] for i in range(2)]
            silu = sb("silu", [P, CW], F32, ff)
            hidden = sb("hidden", [P, T], F32, ff)
        with ExitStack() as pl:
            p_raw = sb("p_raw", [P, PC, T], F32, pl)
            p_hi = sb("p_hi", [P, PC, T], F32R, pl)
            p_lo = sb("p_lo", [P, PC, T], F32R, pl)
            proj = sb("proj", [P, 2, T], F32, pl)
            gate = sb("gate", [P, 2, T], F32, pl)
        with ExitStack() as gm:
            v_tok = sb("v_tok", [P, TT, D], F32, gm)
            u_act = sb("u_act", [P, T], F32, gm)
            mixed = sb("mixed", [P, T], F32, gm)
            vgain = sb("vgain", [P, D], F32, gm)
        with ExitStack() as top:
            sb("conv_room", [P, CONV_ROOM], F32, top)
            w_hi_2 = sb("w_hi_2", [P, KC * WU], F32R, top)
            w_lo_2 = sb("w_lo_2", [P, KC * WU], F32R, top)
        slots_hi = [w_hi_0, [w_hi_1, w_hi_2]]
        slots_lo = [w_lo_0, [w_lo_1, w_lo_2]]

        def w_hi(u):
            return slots_hi[u >= BASE["attn_out"]][u % 2]

        def w_lo(u):
            return slots_lo[u >= BASE["attn_out"]][u % 2]

        psum = ctx.enter_context(nc.psum_tensor("psum", [P, 8, 512], F32))
        flat = psum[:, :, :].rearrange("p b c -> p (b c)")

        NU = len(UNITS)
        FIRST = {name: BASE[name] for name, _ in PH}
        LAST = {name: BASE[name] + len(ks) - 1 for name, ks in PH}
        by_proj = [u for u, (name, _, k) in enumerate(UNITS) if k == PC]
        by_act = [u for u, (name, _, _) in enumerate(UNITS) if name in ("qkv", "gmlp_v")]
        by_dve = [u for u in range(NU) if u not in by_act and u not in by_proj]
        off_part = [sum(PARTS[:q]) for q in range(len(PARTS))]
        up_unit = {(l, off_part[q] + i): FIRST[f"up{l}{q}"] + i
                   for l in range(2) for q, n in enumerate(PARTS) for i in range(n)}

        w_loaded = [sem("w_loaded0"), sem("w_loaded1")]
        w_hi_ready, n_w_hi_ready = sem("w_hi_ready"), counts(range(NU))
        w_lo_ready, n_w_lo_ready = sem("w_lo_ready"), counts(range(NU))
        product, n_product = sem("product"), counts([(u, j) for u in range(NU) for j in range(2)])
        free_act, n_free_act = sem("free_act"), counts([(u, j) for u in by_act for j in range(2)])
        free_dve, n_free_dve = sem("free_dve"), counts([(u, j) for u in by_dve for j in range(2)])
        op_keys = [(s, n) for s in OPERANDS for n in range(KC)]
        op_hi, n_op_hi = sem("op_hi"), counts(op_keys)
        op_lo, n_op_lo = sem("op_lo"), counts(op_keys)
        norm_keys = [(s, n) for s in NORMS for n in range(KC)]
        x_ready, n_x_ready = sem("x_ready"), counts([(s, n) for s in ("mix1", "out") for n in range(KC)])
        squared, n_squared = sem("squared"), counts(norm_keys)
        summed, n_summed = sem("summed"), counts(norm_keys)
        s_x = sem("s_x")
        s_const = sem("s_const")
        s_const_pool = sem("s_const_pool")
        col_sum, n_col_sum = sem("col_sum"), counts(["mix0", "mix1"])
        col_ms, n_col_ms = sem("col_ms"), counts(["mix0", "mix1"])
        col_rms, n_col_rms = sem("col_rms"), counts(["mix0", "mix1"])
        col_inv, n_col_inv = sem("col_inv"), counts(["mix0", "mix1"])
        row_norms = [s for s in NORMS if s != "mix0"]
        row_sum, n_row_sum = sem("row_sum"), counts(row_norms)
        row_rms, n_row_rms = sem("row_rms"), counts(row_norms)
        chain = sem("dve_chain")
        head_sum, n_head_sum = sem("head_sum"), counts(range(5))
        head_rms, n_head_rms = sem("head_rms"), counts(range(5))
        z_done, n_z_done = sem("z_done"), counts(range(9))
        turned, n_turned = sem("turned"), counts([(i, e) for i in range(9) if i != 5 for e in range(2 if i < 8 else 1)])
        turned_out, n_turned_out = sem("turned_out"), counts(list(n_turned))
        s_kvout = sem("s_kvout")
        s_kiout = sem("s_kiout")
        idx_items = [("p", j, h) for j in (1, 2, 3) for h in range(HI)] + [("s", b, c) for b in range(NB) for c in range(3)]
        n_pi = 3 * HI
        idx_ready, n_idx_ready = sem("idx_ready"), counts(range(len(idx_items)))
        relu_ready, n_relu_ready = sem("relu_ready"), counts(range(len(idx_items)))
        summed_heads, n_summed_heads = sem("summed_heads"), counts(range(n_pi))
        s_kidx = [sem("s_kidx0"), sem("s_kidx1")]
        kidx_new, n_kidx_new = sem("kidx_new"), counts(range(NB))
        s_attc = sem("s_attc")
        pool_zero, n_pool_zero = sem("pool_zero"), counts(["w_sel"])
        w_rows_ready, n_w_rows_ready = sem("w_rows_ready"), counts([0])
        w_rows_turned, n_w_rows_turned = sem("w_rows_turned"), counts([0])
        w_sel_ready, n_w_sel_ready = sem("w_sel_ready"), counts([0])
        sel_done, n_sel_done = sem("sel_done"), counts(range(NB))
        score_taken, n_score_taken = sem("score_taken"), counts([0])
        att = [("p", j, h) for j in range(4) for h in range(H)] + [("s", b, 0) for b in range(NB)]
        NA = len(att)
        NPA = NA - NB
        bias_ready, n_bias_ready = sem("bias_ready"), counts(["p0", "p1", "p2", "p3", "s"])
        logits, n_logits = sem("logits"), counts(range(NA))
        neg_max, n_neg_max = sem("neg_max"), counts(range(NA))
        exp_done, n_exp_done = sem("exp_done"), counts(range(NA))
        prob_ready, n_prob_ready = sem("prob_ready"), counts(range(NA))
        pt_ready, n_pt_ready = sem("pt_ready"), counts(range(NA))
        pt_taken, n_pt_taken = sem("pt_taken"), counts(range(NA))
        out_ready, n_out_ready = sem("out_ready"), counts(range(NA))
        out_taken, n_out_taken = sem("out_taken"), counts(range(NA))
        s_key = [sem("s_key0"), sem("s_key1")]
        s_val = [sem("s_val0"), sem("s_val1")]
        key_new, n_key_new = sem("key_new"), counts(range(NB))
        s_spat = [sem("s_spat0"), sem("s_spat1")]
        s_vgain = sem("s_vgain")
        tril, n_tril = sem("tril"), counts(range(KC))
        v_sq, n_v_sq = sem("v_sq"), counts(range(TT))
        v_rms, n_v_rms = sem("v_rms"), counts([0])
        v_norm, n_v_norm = sem("v_norm"), counts(range(TT))
        s_gv = sem("s_gv")
        mix_ready, n_mix_ready = sem("mix_ready"), counts(range(KC))
        mix_taken, n_mix_taken = sem("mix_taken"), counts(range(KC))
        u_gelu, n_u_gelu = sem("u_gelu"), counts(range(KC))
        gated, n_gated = sem("gated"), counts(range(KC))
        cj = [(l, c, j) for l in range(2) for c in range(FC) for j in range(2)]
        cc = [(l, c) for l in range(2) for c in range(FC)]
        s_past = sem("s_past")
        pads, n_pads = sem("pads"), counts(cc)
        tail, n_tail = sem("tail"), counts(cc)
        s_tails = sem("s_tails")
        conv0, n_conv0 = sem("conv0"), counts(cj)
        conv_done, n_conv_done = sem("conv_done"), counts(cj)
        silu_done, n_silu_done = sem("silu_done"), counts(cc)
        h_ready, n_h_ready = sem("h_ready"), counts(cc)
        h_hi, n_h_hi = sem("h_hi"), counts(cc)
        h_lo, n_h_lo = sem("h_lo"), counts(cc)
        nn = [(l, n) for l in range(2) for n in range(KC)]
        s_p = sem("s_p")
        p_hi_ready, n_p_hi_ready = sem("p_hi_ready"), counts(range(2))
        p_lo_ready, n_p_lo_ready = sem("p_lo_ready"), counts(range(2))
        proj_ready, n_proj_ready = sem("proj_ready"), counts(nn)
        gate_done, n_gate_done = sem("gate_done"), counts(nn)
        s_y = sem("s_y")

        block = ctx.enter_context(nc.Block())

        def bank2(j, w):
            return psum[:, 2 * j:2 * j + 2, 0:w]

        def halves(ap):
            return ap.rearrange("p (a t) -> p a t", a=2)

        def seqs(ap):
            return ap.rearrange("p (b q) -> p b q", b=NB)

        def f32(ap):
            return ap.bitcast(F32)

        def padded(ap, n):
            return ap[:, TP:TP + n * (TQ + 2)].rearrange("p (i e) -> p i e", e=TQ + 2)[:, :, 0:2]

        def chunks(width, size=512):
            return [(c, min(size, width - c)) for c in range(0, width, size)]

        def after_projection(eng):
            eng.wait_ge(product, n_product[LAST["qkv"], 1])
            eng.wait_ge(turned_out, len(n_turned_out))
            eng.wait_ge(s_kvout, 64)
            eng.wait_ge(s_kiout, 32)

        @block.sync
        def _(sp):
            def load_unit(u):
                if u >= 2:
                    sp.wait_ge(w_lo_ready, n_w_lo_ready[u - 2])
                n = OFFSET[u + 1] - OFFSET[u]
                sp.dma_start(w_raw[u % 2][:, 0:n // P],
                             weights[OFFSET[u]:OFFSET[u + 1]].rearrange("(p c) -> p c", p=P)).then_inc(w_loaded[u % 2], 16)

            sp.dma_start(xT[:, 0:2, :], xT_in[:, 0:2, :]).then_inc(s_x, 16)
            load_unit(0)
            sp.dma_start(xT[:, 2:KC, :], xT_in[:, 2:KC, :]).then_inc(s_x, 16)
            for u in range(1, FIRST["attn_out"] + 2):
                load_unit(u)
            after_projection(sp)
            sp.dma_start(onehot[:, :], onehot_in).then_inc(s_attc, 16)
            sp.dma_start(qeq[:, :], qeq_in).then_inc(s_attc, 16)
            for b in range(NB):
                if b >= 2:
                    sp.wait_ge(idx_ready, n_idx_ready[n_pi + 3 * (b - 2) + 2])
                sp.dma_start(kidx_b[b % 2][:, 0:PAST], kidxT_in[b]).then_inc(s_kidx[b % 2], 16)
            for b in range(NB):
                if b == 0:
                    sp.wait_ge(idx_ready, len(n_idx_ready))
                if b >= 2:
                    sp.wait_ge(logits, n_logits[NPA + b - 2])
                sp.dma_start(key_b[b % 2][:, :, 0:PAST], keyT_in[b]).then_inc(s_key[b % 2], 16)
                if b >= 2:
                    sp.wait_ge(out_ready, n_out_ready[NPA + b - 2])
                sp.dma_start(val_b[b % 2][:, 0:8, :], val_in[b]).then_inc(s_val[b % 2], 16)
                sp.dma_start(val_b[b % 2][0:TQ, 8, :], vtok[TQ * b:TQ * b + TQ, TT - 1, :]).then_inc(s_val[b % 2], 16)
            done = FIRST["attn_out"] + 2
            for l in range(2):
                if l:
                    sp.wait_ge(pads, n_pads[0, FC - 1])
                    sp.dma_start(pastT[:, :, :], pastT_in[:, 1]).then_inc(s_past, 16)
                first_ple = FIRST[f"ple{l}"]
                for u in range(done, first_ple):
                    if u == FIRST["gmlp_v"] + 2:
                        sp.wait_ge(x_ready, n_x_ready["mix1", KC - 1])
                        sp.dma_start(vgain[:, :], vgain_in).then_inc(s_vgain, 16)
                    load_unit(u)
                    name, i, _ = UNITS[u - 1]
                    if name == "gmlp_u":
                        for n in (2 * i, 2 * i + 1):
                            if n >= 2:
                                sp.wait_ge(mix_ready, n_mix_ready[n - 2])
                                sp.wait_ge(mix_taken, n_mix_taken[n - 2])
                            sp.dma_start(spat[n % 2][:, 0, :], spat_in[:, n, :]).then_inc(s_spat[n % 2], 16)
                            sp.dma_start(spat[n % 2][:, 1, :], spat_s_in[:, n, :]).then_inc(s_spat[n % 2], 16)
                            sp.dma_start(sbias[n % 2][:, :], sbias_in[:, n, :]).then_inc(s_spat[n % 2], 16)
                sp.wait_ge(h_lo, n_h_lo[l, FC - 1])
                sp.wait_ge(tail, n_tail[l, FC - 1])
                sp.dma_start(p_raw[:, :, :], pT_in[:, l]).then_inc(s_p, 16)
                for u in range(first_ple, first_ple + 8):
                    load_unit(u)
                done = first_ple + 8

        def attention_pe(pe):
            after_projection(pe)

            def sel(b):
                pe.wait_ge(relu_ready, n_relu_ready[n_pi + 3 * b + 2])
                for c, (k0, w) in enumerate(chunks(KEYS)):
                    last = pe.matmul(psum[:, 4 + c, 0:w], w_sel[:, P * b:P * b + P], probs[b % 2][:, k0:k0 + w],
                                     start=(b == 0), stop=(b == NB - 1))
                last.then_inc(sel_done, 1)

            for n, (kind, a, c) in enumerate(idx_items):
                if n >= 4:
                    pe.wait_ge(relu_ready, n_relu_ready[n - 4])
                if kind == "p":
                    half = DI * (c % 2)
                    pe.matmul(psum[:, n % 4, 0:P * (a + 1)], qiT[half:half + DI, c // 2, P * a:P * a + P],
                              kiT[half:half + DI, 0:P * (a + 1)], start=True, stop=True).then_inc(idx_ready, 1)
                    if n == 8:
                        pe.wait_ge(w_rows_ready, n_w_rows_ready[0])
                        pe.transpose(psum[:, 7, 0:P], w_rows[:, :], ident[:, :]).then_inc(w_rows_turned, 1)
                else:
                    if c == 0:
                        pe.wait_ge(s_kidx[a % 2], 16 * (a // 2 + 1))
                        pe.wait_ge(kidx_new, n_kidx_new[a])
                    k0, w = chunks(KEYS)[c]
                    pe.matmul(psum[:, n % 4, 0:w], qi_blk[:, a, :], kidx_b[a % 2][:, k0:k0 + w],
                              start=True, stop=True).then_inc(idx_ready, 1)
                    if c == 2 and a >= 1:
                        if a == 1:
                            pe.wait_ge(w_sel_ready, n_w_sel_ready[0])
                        sel(a - 1)
            sel(NB - 1)

            def scores(s):
                kind, a, h = att[s]
                if kind == "p":
                    if s >= 3:
                        pe.wait_ge(exp_done, n_exp_done[s - 3])
                    else:
                        pe.wait_ge(relu_ready, len(n_relu_ready))
                    if h == 0:
                        pe.wait_ge(bias_ready, n_bias_ready[f"p{a}"])
                    w = P * (a + 1)
                    pe.matmul(psum[:, s % 3, 0:w], ident_b[:, :], bias_p[a][:, :], start=True, stop=False)
                    pe.matmul(psum[:, s % 3, 0:w], qT[:, h, P * a:P * a + P], kT[:, h // R, 0:w],
                              start=False, stop=True).then_inc(logits, 1)
                    return
                pe.wait_ge(exp_done, n_exp_done[s - 1])
                if a == 0:
                    pe.wait_ge(bias_ready, n_bias_ready["s"])
                pe.wait_ge(s_key[a % 2], 16 * (a // 2 + 1))
                pe.wait_ge(key_new, n_key_new[a])
                for c, (k0, w) in enumerate(chunks(KEYS)):
                    pe.matmul(psum[:, c, 0:w], onehot[:, P * a:P * a + P], bias_s[:, k0:k0 + w],
                              start=True, stop=False, skip_group_check=True)
                    for g in range(G):
                        last = pe.matmul(psum[64 * g:64 * g + 64, c, 0:w],
                                         q_smp[:, a, 64 * g:64 * g + 64],
                                         key_b[a % 2][:, g, k0:k0 + w], start=False, stop=True, skip_group_check=True)
                last.then_inc(logits, 1)

            def turn_probs(s):
                kind, a, h = att[s]
                pe.wait_ge(prob_ready, n_prob_ready[s])
                if kind == "p":
                    if s >= 3:
                        pe.wait_ge(pt_taken, n_pt_taken[s - 3])
                    for i in range(a + 1):
                        last = pe.transpose(psum[:, 3 + s % 3, P * i:P * i + P], probs[s % 2][:, P * i:P * i + P], ident[:, :])
                else:
                    pe.wait_ge(pt_taken, n_pt_taken[s - 1])
                    for i in range(9):
                        m = P if i < 8 else TQ
                        last = pe.transpose(flat[0:m, 1536 + P * i:1536 + P * i + P], probs[s % 2][:, P * i:P * i + m],
                                            ident[:, :])
                last.then_inc(pt_ready, 1)

            def weigh(s):
                kind, a, h = att[s]
                pe.wait_ge(pt_taken, n_pt_taken[s])
                if s >= 2:
                    pe.wait_ge(out_taken, n_out_taken[s - 2])
                o = psum[:, 6 + s % 2, :]
                if kind == "p":
                    for i in range(a + 1):
                        last = pe.matmul(o[:, 0:P], vtok[:, i, P * (h // R):P * (h // R) + P],
                                         probsT[s % 2][:, i, :], start=(i == 0), stop=(i == a))
                else:
                    pe.wait_ge(s_val[a % 2], 32 * (a // 2 + 1))
                    for g in range(G):
                        for i in range(9):
                            m = P if i < 8 else TQ
                            last = pe.matmul(o[:, 64 * g:64 * g + 64], val_b[a % 2][0:m, i, P * g:P * g + P],
                                             probsT[s % 2][0:m, i, 64 * g:64 * g + 64], start=(i == 0), stop=(i == 8))
                last.then_inc(out_ready, 1)

            pe.wait_ge(score_taken, n_score_taken[0])
            scores(0)
            for s in range(NA + 2):
                if 1 <= s <= NA:
                    turn_probs(s - 1)
                if s >= 2:
                    weigh(s - 2)
                if s + 1 < NA:
                    scores(s + 1)

        @block.tensor
        def _(pe):
            def free(u, j):
                if u - 1 in by_proj:
                    pe.wait_ge(proj_ready, n_proj_ready[int(UNITS[u - 1][0][3]), UNITS[u - 1][1] + j])
                elif u - 1 in by_act:
                    pe.wait_ge(free_act, n_free_act[u - 1, j])
                elif u >= 1:
                    pe.wait_ge(free_dve, n_free_dve[u - 1, j])

            def product_b(u, hi, lo, split, ready=None):
                K = UNITS[u][2]
                wh = w_hi(u)[:, 0:K * WU].rearrange("p (k c) -> p k c", k=K)
                wl = w_lo(u)[:, 0:K * WU].rearrange("p (k c) -> p k c", k=K)
                pe.wait_ge(w_lo_ready, n_w_lo_ready[u])
                for j in range(2):
                    free(u, j)
                    for k in range(K):
                        if ready and j == 0:
                            ready(k)
                        for n, (w, x) in enumerate(((wh, hi), (wh, lo), (wl, hi))):
                            for bank, t0, t1 in ((0, 0, split), (1, split, T)):
                                last = pe.matmul(psum[:, 2 * j + bank, 0:t1 - t0], w[:, k, P * j:P * j + P],
                                                 x[:, k, t0:t1], start=(k == 0 and n == 0),
                                                 stop=(k == K - 1 and n == 2))
                    last.then_inc(product, 1)
                    extra(u, j)

            def product_a(u, hi, lo, ready=None):
                w = WIDTH[u]
                wh = w_hi(u)[:, 0:KC * w].rearrange("p (k c) -> p k c", k=KC)
                wl = w_lo(u)[:, 0:KC * w].rearrange("p (k c) -> p k c", k=KC)
                pe.wait_ge(w_lo_ready, n_w_lo_ready[u])
                for j, tiles in enumerate((range(4), (4,))):
                    free(u, j)
                    for t in tiles:
                        out = psum[:, 2 * j + t % 4 // 2, WU * (t % 2):WU * (t % 2) + w]
                        for k in range(KC):
                            if ready and t == 0:
                                ready(k)
                            for n, (x, ww) in enumerate(((hi, wh), (hi, wl), (lo, wh))):
                                last = pe.matmul(out, x[:, k, P * t:P * t + P], ww[:, k, :],
                                                 start=(k == 0 and n == 0), stop=(k == KC - 1 and n == 2))
                    last.then_inc(product, 1)
                    extra(u, j)

            def row_stats(norm):
                pe.wait_ge(summed, n_summed[norm, KC - 1])
                for i in range(2):
                    last = pe.matmul(psum[:, 6 + i, 0:T // 2], ones[:, :], square_sum[:, i * T // 2:(i + 1) * T // 2],
                                     start=True, stop=True)
                last.then_inc(row_sum, 1)

            def col_stats(norm):
                pe.wait_ge(summed, n_summed[norm, KC - 1])
                for t in range(TT):
                    last = pe.matmul(psum[:, 5, t:t + 1], square_sum[:, P * t:P * t + P], ones[:, 0:1],
                                     start=True, stop=True)
                last.then_inc(col_sum, 1)

            def turn(i):
                pe.wait_ge(z_done, n_z_done[i])
                if i == 0:
                    pe.wait_ge(col_ms, n_col_ms["mix0"])
                for e in range(2 if i < 8 else 1):
                    prev = list(n_turned).index((i, e)) - 2
                    if prev >= 0:
                        pe.wait_ge(turned_out, n_turned_out[list(n_turned)[prev]])
                    slot = list(n_turned).index((i, e)) % 2
                    for t in range(TT):
                        last = pe.transpose(flat[:, 2048 + 1024 * slot + P * t:2048 + 1024 * slot + P * t + P],
                                            z[i % 2][:, t, P * e:P * e + P], ident[:, :])
                    last.then_inc(turned, 1)

            def extra(u, j):
                name, i, _ = UNITS[u]
                if name == "qkv" and j == 0:
                    if i == 0:
                        col_stats("mix0")
                    elif i - 1 != 5:
                        turn(i - 1)
                if name == "gmlp_v" and i == 0 and j == 0:
                    col_stats("mix1")
                    row_stats("mix1")
                if name in ("up00", "up10") and i == 0 and j == 0:
                    row_stats(f"ffn{name[2]}")
                if name[:3] == "ple" and i == 0 and j == 1:
                    row_stats(name)
                if name == "gmlp_u":
                    n = 2 * i + j
                    if n >= 1:
                        mix(n - 1)
                    if n == KC - 1:
                        mix(n)

            def mix(n):
                if n == 0:
                    pe.wait_ge(row_rms, n_row_rms["mix1"])
                    pe.wait_ge(v_norm, len(n_v_norm))
                if n >= 2:
                    pe.wait_ge(mix_taken, n_mix_taken[n - 2])
                pe.wait_ge(tril, n_tril[n])
                for t in range(TT):
                    o = 2048 + 1024 * (n % 2) + P * t
                    last = pe.matmul(flat[:, o:o + P], v_tok[:, t, P * n:P * n + P], spat[n % 2][:, t // 4, :],
                                     start=True, stop=True)
                last.then_inc(mix_ready, 1)

            def operand(stage):
                return lambda k: pe.wait_ge(op_lo, n_op_lo[stage, k])

            pe.wait_ge(s_const, 16 * 6)
            pe.wait_ge(s_const_pool, 2)
            for i in range(9):
                product_a(i, a_hi_0, a_lo_0, operand("mix0") if i == 0 else None)
            turn(8)
            attention_pe(pe)
            for i in range(4):
                product_b(FIRST["attn_out"] + i, a_hi, a_lo, T // 2, operand("attn") if i == 0 else None)
            for l in range(2):
                if l:
                    for i in range(4):
                        product_a(FIRST["gmlp_v"] + i, g_hi, g_lo, operand("mix1") if i == 0 else None)
                    for i in range(4):
                        product_b(FIRST["gmlp_u"] + i, g_hi, g_lo, T // 2)
                    for i in range(4):
                        product_b(FIRST["gmlp_out"] + i, a_hi, a_lo, T // 2, operand("gate") if i == 0 else None)
                for q, n in enumerate(PARTS):
                    for i in range(n):
                        product_b(FIRST[f"up{l}{q}"] + i, a_hi, a_lo, 256,
                                  operand(f"ffn{l}") if q == i == 0 else None)
                    for i in range(4):
                        product_b(FIRST[f"down{l}{q}"] + i, g_hi, g_lo, T // 2,
                                  (lambda k: pe.wait_ge(h_lo, n_h_lo[l, off_part[q] + k])) if i == 0 else None)
                for i in range(4):
                    u = FIRST[f"ple{l}"] + 2 * i
                    if i == 0:
                        pe.wait_ge(p_lo_ready, n_p_lo_ready[l])
                    product_b(u, p_hi, p_lo, T // 2)
                    product_b(u + 1, a_hi, a_lo, T // 2, operand(f"ple{l}") if i == 0 else None)

        def attention_act(act, split_hi):
            after_projection(act)
            split_hi(FIRST["attn_out"])
            for n, (kind, a, c) in enumerate(idx_items):
                if kind == "p":
                    act.wait_ge(idx_ready, n_idx_ready[n])
                    if n >= 2:
                        act.wait_ge(summed_heads, n_summed_heads[n - 2])
                    w = P * (a + 1)
                    act.activation(probs[n % 2][:, 0:w], psum[:, n % 4, 0:w], ACT.Relu, scale=DI ** -0.5)\
                       .then_inc(relu_ready, 1)
                    continue
                if c == 0:
                    if a < 2:
                        act.wait_ge(summed_heads, len(n_summed_heads))
                    else:
                        act.wait_ge(sel_done, n_sel_done[a - 2])
                act.wait_ge(idx_ready, n_idx_ready[n])
                k0, w = chunks(KEYS)[c]
                act.activation(probs[a % 2][:, k0:k0 + w], psum[:, n % 4, 0:w], ACT.Relu, scale=DI ** -0.5)\
                   .then_inc(relu_ready, 1)
            act.wait_ge(sel_done, len(n_sel_done))
            act.activation(score_s[:, :], flat[:, 2048:2048 + KEYS], ACT.Copy).then_inc(score_taken, 1)

            def turn_out_probs(s):
                kind, a, h = att[s]
                act.wait_ge(pt_ready, n_pt_ready[s])
                if s >= 2:
                    act.wait_ge(out_ready, n_out_ready[s - 2])
                if kind == "p":
                    w = a + 1
                    src = psum[:, 3 + s % 3, 0:P * w].rearrange("p (i r) -> p i r", r=P)
                    act.activation(probsT[s % 2][:, 0:w, :], src, ACT.Copy).then_inc(pt_taken, 1)
                else:
                    act.activation(probsT[s % 2][:, 0:8, :], flat[:, 1536:2560].rearrange("p (i r) -> p i r", r=P), ACT.Copy)
                    act.activation(probsT[s % 2][0:TQ, 8, :], flat[0:TQ, 2560:2688], ACT.Copy).then_inc(pt_taken, 1)

            def take_out(s):
                kind, a, h = att[s]
                act.wait_ge(out_ready, n_out_ready[s])
                o = psum[:, 6 + s % 2, 0:P]
                if kind == "p":
                    last = act.activation(qT[:, h, P * a:P * a + P], o, ACT.Copy)
                else:
                    last = act.activation(qT[:, :, TP + TQ * a:TP + TQ * a + TQ], o.rearrange("p (h q) -> p h q", q=TQ),
                                          ACT.Copy)
                last.then_inc(out_taken, 1)

            for s in range(NA + 2):
                if s < NA:
                    kind, a, h = att[s]
                    w = P * (a + 1) if kind == "p" else KEYS
                    src = psum[:, s % 3, 0:w] if kind == "p" else flat[:, 0:w]
                    act.wait_ge(neg_max, n_neg_max[s])
                    if s >= 2:
                        act.wait_ge(pt_ready, n_pt_ready[s - 2])
                    act.activation(probs[s % 2][:, 0:w], src, ACT.Exp, bias=stat[:, 1, s:s + 1], scale=SCALE,
                                   accum_out=stat[:, 2, s:s + 1]).then_inc(exp_done, 1)
                if 1 <= s <= NA:
                    turn_out_probs(s - 1)
                if s >= 2:
                    take_out(s - 2)

        def gated_mlp_act(act, split_hi, root_col, root_row, operand_hi, square_x):
            for i in range(4):
                u = FIRST["gmlp_v"] + i
                split_hi(u + 1)
                if i == 0:
                    root_col("mix1")
                    root_row("mix1")
                    act.wait_ge(col_inv, n_col_inv["mix1"])
                for j, tiles in enumerate((range(4), (4,))):
                    act.wait_ge(product, n_product[u, j])
                    for t in tiles:
                        last = act.activation(v_tok[:, t, WU * i:WU * i + WU],
                                              psum[:, 2 * j + t % 4 // 2, WU * (t % 2):WU * (t % 2) + WU],
                                              ACT.Gelu_apprx_tanh, scale=rcol[:, 4, t:t + 1])
                    last.then_inc(free_act, 1)
            act.wait_ge(summed, n_summed["mix1", KC - 1])
            act.wait_ge(free_act, n_free_act[LAST["gmlp_v"], 1])
            junk = square[:, :, :].rearrange("p a t -> p (a t)")[:, 0:D]
            for t in range(TT):
                if t:
                    act.wait_ge(v_sq, n_v_sq[t - 1])
                act.activation(junk, v_tok[:, t, :], ACT.Square, accum_out=rcol[:, 5, t:t + 1]).then_inc(v_sq, 1)
            act.wait_ge(v_sq, len(n_v_sq))
            act.activation(rcol[:, 6, :], rcol[:, 5, :], ACT.Sqrt, bias=eps[:, 0:1], scale=1.0 / D).then_inc(v_rms, 1)
            for i in range(4):
                split_hi(FIRST["gmlp_u"] + i + 1)
                for n in (2 * i, 2 * i + 1):
                    act.wait_ge(free_dve, n_free_dve[FIRST["gmlp_u"] + i, n % 2])
                    act.activation(u_act[:, :], u_act[:, :], ACT.Gelu_apprx_tanh).then_inc(u_gelu, 1)
                    act.wait_ge(gated, n_gated[n])
                    operand_hi("gate", n, a_hi, u_act[:, :])
            for i in range(4):
                split_hi(FIRST["gmlp_out"] + i + 1)
                for n in (2 * i, 2 * i + 1):
                    act.wait_ge(free_dve, n_free_dve[FIRST["gmlp_out"] + i, n % 2])
                    square_x("ffn1", n)
            act.wait_ge(product, n_product[LAST["gmlp_out"], 1])
            for n in range(KC):
                operand_hi("ffn1", n, a_hi, xT[:, n, :], 4)

        @block.scalar
        def _(act):
            for dst, src in ((gains[:, :, :], gains_in), (qkgain[:, :, :], qkgain_in), (rope[:, :, :], rope_in),
                             (ident[:, :], ident_in), (convw[:, :, :, :], convw_in)):
                act.dma_start(dst, src).then_inc(s_const, 16)
            act.dma_start(pastT[:, :, :], pastT_in[:, 0]).then_inc(s_past, 16)

            def split_hi(u):
                if u >= NU:
                    return
                n = (OFFSET[u + 1] - OFFSET[u]) // P
                act.wait_ge(w_loaded[u % 2], 16 * (u // 2 + 1))
                if u >= 2:
                    act.wait_ge(product, n_product[u - 2, 1])
                act.activation(w_hi(u)[:, 0:n], w_raw[u % 2][:, 0:n], ACT.Copy).then_inc(w_hi_ready, 1)

            def operand_hi(stage, n, dst, src, gain=None):
                act.activation(dst[:, n, :], src, ACT.Copy, scale=1.0 if gain is None else gains[:, gain, n:n + 1])\
                   .then_inc(op_hi, 1)

            def square_x(norm, n):
                k = norm_keys.index((norm, n))
                if k >= 2:
                    act.wait_ge(summed, n_summed[norm_keys[k - 2]])
                act.activation(square[:, k % 2, :], xT[:, n, :], ACT.Square).then_inc(squared, 1)

            def root_row(norm):
                act.wait_ge(row_sum, n_row_sum[norm])
                act.activation(rms[:, :].rearrange("p (a t) -> p a t", a=2), psum[:, 6:8, 0:T // 2], ACT.Sqrt,
                               bias=eps[:, 0:1], scale=1.0 / D).then_inc(row_rms, 1)

            def root_col(norm):
                act.wait_ge(col_ms, n_col_ms[norm])
                act.activation(rcol[:, 1, :], rcol[:, 0, :], ACT.Sqrt).then_inc(col_rms, 1)

            act.wait_ge(s_const_pool, 3)
            act.wait_ge(s_const, 16 * 5)
            act.wait_ge(s_x, 32)
            act.activation(ident_b[:, :], ident[:, :], ACT.Copy).then_inc(s_const, 16)
            for n in range(KC):
                operand_hi("mix0", n, a_hi_0, xT[:, n, :], 0)
                square_x("mix0", n)
                if n == 0:
                    split_hi(0)

            def project(i):
                if i < 8:
                    split_hi(i + 1)
                if i == 0:
                    root_col("mix0")
                    act.wait_ge(col_inv, n_col_inv["mix0"])
                dst = vtok if i == 5 else z[i % 2]
                if i >= 2 and i - 2 != 5:
                    act.wait_ge(turned, n_turned[i - 2, 1])
                if i == 6:
                    act.wait_ge(s_kvout, 64)
                w = WIDTH[i]
                for j, tiles in enumerate((range(4), (4,))):
                    act.wait_ge(product, n_product[i, j])
                    for t in tiles:
                        last = act.activation(dst[:, t, 0:w],
                                              psum[:, 2 * j + t % 4 // 2, WU * (t % 2):WU * (t % 2) + w],
                                              ACT.Copy, scale=rcol[:, 4, t:t + 1])
                    last.then_inc(free_act, 1)
                if i < 5:
                    act.wait_ge(head_sum, n_head_sum[i])
                    act.activation(hstat[:, 1, :], hstat[:, 0, :], ACT.Sqrt, bias=eps[:, 0:1], scale=1.0 / P)\
                       .then_inc(head_rms, 1)

            def turn_out(i):
                for e in range(2 if i < 8 else 1):
                    act.wait_ge(turned, n_turned[i, e])
                    o = 2048 + 1024 * (list(n_turned).index((i, e)) % 2)
                    src = flat[:, o:o + T]
                    if i < 4:
                        h = 2 * i + e
                        act.activation(qT[:, h, 0:TP], src[:, 0:TP], ACT.Copy)
                        last = act.activation(q_smp[:, :, TQ * h:TQ * h + TQ], seqs(src[:, TP:T]), ACT.Copy)
                    elif i == 4:
                        last = act.activation(kT[:, e, :], src, ACT.Copy)
                    elif i < 8:
                        pair = 2 * (i - 6) + e
                        act.activation(qiT[:, pair, :], src[:, 0:TP], ACT.Copy)
                        for half in range(2):
                            a, c = DI * half, DI * half + TQ * pair
                            last = act.activation(qi_blk[a:a + DI, :, c:c + TQ], seqs(src[a:a + DI, TP:T]), ACT.Copy)
                    else:
                        last = act.activation(kiT[:, :], src, ACT.Copy)
                    last.then_inc(turned_out, 1)

            for i in range(9):
                project(i)
                if i >= 1 and i - 1 != 5:
                    turn_out(i - 1)
            turn_out(8)
            attention_act(act, split_hi)
            act.wait_ge(out_taken, len(n_out_taken))
            for n in range(KC):
                operand_hi("attn", n, a_hi, qT[:, n, :])

            for i in range(4):
                split_hi(FIRST["attn_out"] + i + 1)
                for n in (2 * i, 2 * i + 1):
                    act.wait_ge(free_dve, n_free_dve[FIRST["attn_out"] + i, n % 2])
                    square_x("ffn0", n)
            act.wait_ge(product, n_product[LAST["attn_out"], 1])
            for n in range(KC):
                operand_hi("ffn0", n, a_hi, xT[:, n, :], 1)
            for l in range(2):
                if l:
                    gated_mlp_act(act, split_hi, root_col, root_row, operand_hi, square_x)
                for q, np_ in enumerate(PARTS):
                    for i in range(np_):
                        c = off_part[q] + i
                        split_hi(FIRST[f"up{l}{q}"] + i + 1)
                        if q == i == 0:
                            root_row(f"ffn{l}")
                        ci, co = conv_in[c % 2], conv[c % 2]
                        act.wait_ge(pads, n_pads[l, c])
                        if c >= 2:
                            act.wait_ge(h_ready, n_h_ready[l, c - 2])
                        for j in range(2):
                            act.wait_ge(free_dve, n_free_dve[FIRST[f"up{l}{q}"] + i, j])
                            ch = j * FC + c
                            act.activation(co[j][:, :], ci[j][:, 2:2 + CW], ACT.Identity,
                                           bias=convw[:, l, ch, 3:4], scale=convw[:, l, ch, 2:3])\
                               .then_inc(conv0, 1)
                        act.wait_ge(conv_done, n_conv_done[l, c, 0])
                        if c >= 1:
                            act.wait_ge(h_ready, n_h_ready[l, c - 1])
                        act.activation(silu[:, :], co[0][:, :], ACT.Silu).then_inc(silu_done, 1)
                        act.wait_ge(h_ready, n_h_ready[l, c])
                        if i == 0 and q:
                            act.wait_ge(product, n_product[LAST[f"down{l}{q - 1}"], 1])
                        if i == 0 and not q and l:
                            act.wait_ge(product, n_product[LAST["gmlp_u"], 1])
                        act.activation(g_hi[:, i, :], hidden[:, :], ACT.Copy).then_inc(h_hi, 1)
                    for i in range(4):
                        split_hi(FIRST[f"down{l}{q}"] + i + 1)
                        if q == len(PARTS) - 1:
                            for n in (2 * i, 2 * i + 1):
                                act.wait_ge(free_dve, n_free_dve[FIRST[f"down{l}{q}"] + i, n % 2])
                                square_x(f"ple{l}", n)
                                if n == 0:
                                    act.wait_ge(product, n_product[LAST[f"up{l}{q}"], 1])
                                operand_hi(f"ple{l}", n, a_hi, xT[:, n, :], 2 if l == 0 else 5)
                act.wait_ge(s_p, 16 * (l + 1))
                act.activation(p_hi[:, :, :], p_raw[:, :, :], ACT.Copy).then_inc(p_hi_ready, 1)
                for i in range(4):
                    u = FIRST[f"ple{l}"] + 2 * i
                    split_hi(u + 1)
                    for j in range(2):
                        act.wait_ge(product, n_product[u, j])
                        if i == 0 and j == 0:
                            act.wait_ge(h_lo, n_h_lo[l, FC - 1])
                        if i >= 1:
                            act.wait_ge(x_ready, n_x_ready["mix1" if l == 0 else "out", 2 * i - 2 + j])
                        act.activation(halves(proj[:, j, :]), bank2(j, T // 2), ACT.Copy).then_inc(proj_ready, 1)
                    if i == 0:
                        root_row(f"ple{l}")
                    split_hi(u + 2)
                    for j in range(2):
                        act.wait_ge(free_dve, n_free_dve[u + 1, j])
                        act.activation(gate[:, j, :], gate[:, j, :], ACT.Sigmoid).then_inc(gate_done, 1)
                    if l == 0:
                        for n in (2 * i, 2 * i + 1):
                            act.wait_ge(x_ready, n_x_ready["mix1", n])
                            square_x("mix1", n)
                            if n == 0:
                                act.wait_ge(product, n_product[LAST["down02"], 1])
                            operand_hi("mix1", n, g_hi, xT[:, n, :], 3)

        def padded18(ap):
            return ap[:, 2 + TP:2 + TP + NB * (TQ + 2)].rearrange("p (b e) -> p b e", e=TQ + 2)[:, :, 2:2 + TQ]

        def padded16(ap):
            return ap[:, TP + 2 - 2:TP + NB * (TQ + 2)].rearrange("p (b e) -> p b e", e=TQ + 2)[:, :, 2:TQ + 2]

        def attention_dve(dve, link, split_lo):
            after_projection(dve)
            split_lo(FIRST["attn_out"])
            dve.wait_ge(s_attc, 32)
            for par in range(2):
                last = dve.tensor_tensor(w_rows[:, 64 * par:64 * par + 64].rearrange("p (h q) -> p h q", q=TQ),
                                         qeq[:, :].unsqueeze(1).broadcast_to([P, 4, TQ]),
                                         wi[:, TT - 1, :].rearrange("p (h e) -> p e h", e=2)[:, par, :].unsqueeze(2).broadcast_to([P, 4, TQ]),
                                         ALU.mult)
            last.then_inc(w_rows_ready, 1)
            for n in range(n_pi):
                _, j, h = idx_items[n]
                dve.wait_ge(relu_ready, n_relu_ready[n])
                w = P * (j + 1)
                src, acc, wcol = probs[n % 2][:, 0:w], score_p[j][:, :], wi[:, j, h:h + 1]
                if h == 0:
                    ins = dve.tensor_scalar(acc, src, wcol, None, ALU.mult)
                else:
                    dve.wait_ge(summed_heads, n_summed_heads[n - 1])
                    ins = dve.scalar_tensor_tensor(out=acc, in0=src, scalar=wcol, in1=acc, op0=ALU.mult, op1=ALU.add)
                ins.then_inc(summed_heads, 1)
                if n == 9:
                    dve.wait_ge(w_rows_turned, n_w_rows_turned[0])
                    dve.wait_ge(pool_zero, n_pool_zero["w_sel"])
                    dve.tensor_copy(w_sel[:, :].rearrange("p (b e) -> p b e", e=P + TQ)[:, :, 0:TQ],
                                    seqs(psum[:, 7, 0:P])).then_inc(w_sel_ready, 1)
            dve.wait_ge(summed_heads, len(n_summed_heads))
            for j in range(1, 4):
                last = dve.memset(score_p[j][0:64, P * j + 64:P * j + P], NEG)
            link(last)

            dve.wait_ge(summed_heads, len(n_summed_heads))

            def prompt_round():
                for j in range(1, 4):
                    last = dve.max(best[:, j, :], score_p[j][:, :])
                link(last)
                for j in range(1, 4):
                    last = dve.match_replace(score_p[j][:, :], best[:, j, :], score_p[j][:, :], TAKEN)
                link(last)

            def sample_round():
                link(dve.max(best[:, 0, :], score_s[:, :]))
                link(dve.match_replace(score_s[:, :], best[:, 0, :], score_s[:, :], TAKEN))

            def normed(s):
                kind, a, h = att[s]
                w = P * (a + 1) if kind == "p" else KEYS
                dve.wait_ge(exp_done, n_exp_done[s])
                link(dve.reciprocal(stat[:, 3, s:s + 1], stat[:, 2, s:s + 1]))
                pr = probs[s % 2][:, 0:w]
                dve.tensor_scalar(pr, pr, stat[:, 3, s:s + 1], None, ALU.mult).then_inc(prob_ready, 1)

            def row_max(s):
                kind, a, h = att[s]
                src = psum[:, s % 3, 0:P * (a + 1)] if kind == "p" else flat[:, 0:KEYS]
                dve.wait_ge(logits, n_logits[s])
                link(dve.tensor_reduce(stat[:, 0, s:s + 1], src, AX, ALU.max))
                dve.tensor_scalar(stat[:, 1, s:s + 1], stat[:, 0, s:s + 1], -SCALE, None, ALU.mult).then_inc(neg_max, 1)

            link(dve.memset(bias_p[0][:, :], 0.0))
            dve.memset(bias_p[0][0:64, 64:P], NEG).then_inc(bias_ready, 1)
            R_P, R_S = TOPK_P // 8, TOPK_S // 8
            for r in range(R_P):
                prompt_round()
                s = r - (R_P - H)
                if s >= 1:
                    normed(s - 1)
                if s >= 0:
                    row_max(s)
            for j in range(1, 4):
                link(dve.tensor_scalar(bias_p[j][:, :], score_p[j][:, :], TAKEN / 2, NEG, ALU.is_gt, ALU.mult))
            for j in range(1, 4):
                dve.memset(bias_p[j][0:64, P * j + 64:P * j + P], NEG).then_inc(bias_ready, 1)
            done = 0
            for s in range(H, NA + 1):
                normed(s - 1)
                if s == NA:
                    break
                row_max(s)
                while done < R_S and done * (NPA - H - 1) < (s - H + 1) * R_S and s < NPA - 1:
                    sample_round()
                    done += 1
                if s == NPA - 2:
                    assert done == R_S
                    dve.tensor_scalar(bias_s[:, :], score_s[:, :], TAKEN / 2, NEG, ALU.is_gt, ALU.mult)\
                       .then_inc(bias_ready, 1)

        @block.vector
        def _(dve):
            links = [0]

            def link(ins):
                links[0] += 1
                ins.then_inc(chain, 1)
                dve.wait_ge(chain, links[0])

            def split_lo(u):
                if u >= NU:
                    return
                n = (OFFSET[u + 1] - OFFSET[u]) // P
                dve.wait_ge(w_hi_ready, n_w_hi_ready[u])
                dve.tensor_tensor(w_lo(u)[:, 0:n], w_raw[u % 2][:, 0:n], f32(w_hi(u)[:, 0:n]), ALU.subtract)\
                   .then_inc(w_lo_ready, 1)

            def operand_lo(stage, n, hi, lo, src, gain=None):
                dve.wait_ge(op_hi, n_op_hi[stage, n])
                dve.scalar_tensor_tensor(out=lo[:, n, :], in0=src, scalar=1.0 if gain is None else gains[:, gain, n:n + 1],
                                         in1=f32(hi[:, n, :]), op0=ALU.mult, op1=ALU.subtract).then_inc(op_lo, 1)

            def inverse_col(norm):
                dve.wait_ge(col_sum, n_col_sum[norm])
                dve.tensor_scalar(rcol[:, 0, :], psum[:, 5, 0:TT], 1.0 / D, EPS, ALU.mult, ALU.add).then_inc(col_ms, 1)
                dve.wait_ge(col_rms, n_col_rms[norm])
                link(dve.reciprocal(rcol[:, 2, :], rcol[:, 1, :]))
                link(dve.tensor_tensor(rcol[:, 3, :], rcol[:, 2, :], rcol[:, 2, :], ALU.mult))
                link(dve.tensor_tensor(rcol[:, 3, :], rcol[:, 3, :], rcol[:, 0, :], ALU.mult))
                link(dve.tensor_scalar(rcol[:, 3, :], rcol[:, 3, :], -0.5, 1.5, ALU.mult, ALU.add))
                dve.tensor_tensor(rcol[:, 4, :], rcol[:, 2, :], rcol[:, 3, :], ALU.mult).then_inc(col_inv, 1)

            def inverse_row(norm):
                dve.wait_ge(row_rms, n_row_rms[norm])
                link(dve.reciprocal(inv_rms[:, :], rms[:, :]))

            dve.wait_ge(s_const, 16 * 5)
            dve.wait_ge(s_x, 32)
            for n in range(KC):
                operand_lo("mix0", n, a_hi_0, a_lo_0, xT[:, n, :], 0)
                if n == 0:
                    split_lo(0)

            def rotate(zz, heads, width, half, tab, copies=1):
                zv = zz[:, :, 0:heads * width].rearrange("p t (h d) -> p t h d", d=width)
                x1, x2 = zv[:, :, :, 0:half], zv[:, :, :, half:2 * half]
                n = heads * half
                tmp = [zs[:, :, m * 64:m * 64 + n].rearrange("p t (h d) -> p t h d", d=half) for m in range(4)]
                cos = rope[:, :, tab:tab + half].unsqueeze(2).broadcast_to([P, TT, heads, half])
                sin = rope[:, :, tab + half:tab + 2 * half].unsqueeze(2).broadcast_to([P, TT, heads, half])
                dve.tensor_tensor(tmp[0], x1, cos, ALU.mult)
                dve.tensor_tensor(tmp[1], x2, sin, ALU.mult)
                dve.tensor_tensor(tmp[2], x2, cos, ALU.mult)
                link(dve.tensor_tensor(tmp[3], x1, sin, ALU.mult))
                dve.tensor_tensor(x1, tmp[0], tmp[1], ALU.subtract)
                return dve.tensor_tensor(x2, tmp[2], tmp[3], ALU.add)

            def project(i):
                if i < 8:
                    split_lo(i + 1)
                if i == 0:
                    inverse_col("mix0")
                dve.wait_ge(free_act, n_free_act[i, 1])
                zz = z[i % 2]
                if i < 5:
                    zh = zz[:, :, :].rearrange("p t (h d) -> p (t h) d", d=P)
                    sh = zs[:, :, :].rearrange("p t (h d) -> p (t h) d", d=P)
                    link(dve.tensor_tensor(sh, zh, zh, ALU.mult))
                    dve.tensor_reduce(hstat[:, 0, :], sh, AX, ALU.add).then_inc(head_sum, 1)
                    dve.wait_ge(head_rms, n_head_rms[i])
                    link(dve.reciprocal(hstat[:, 2, :], hstat[:, 1, :]))
                    link(dve.tensor_tensor(sh, zh, hstat[:, 2, :].unsqueeze(2).broadcast_to([P, 2 * TT, P]), ALU.mult))
                    link(dve.tensor_tensor(zh, sh, qkgain[:, i // 4, :].unsqueeze(1).broadcast_to([P, 2 * TT, P]), ALU.mult))
                    rotate(zz, 2, P, 16, 0).then_inc(z_done, 1)
                elif i == 5:
                    dve.tensor_copy(hstat[:, 0, 0:1], hstat[:, 1, 0:1]).then_inc(z_done, 1)
                elif i < 8:
                    rotate(zz, 4, DI, 8, 32).then_inc(z_done, 1)
                else:
                    link(dve.tensor_scalar(wi[:, :, :], zz[:, :, DI:DI + HI], float(HI) ** -0.5, None, ALU.mult))
                    link(rotate(zz, 1, DI, 8, 32))
                    dve.tensor_copy(zz[:, :, DI:2 * DI], zz[:, :, 0:DI]).then_inc(z_done, 1)

            for i in range(9):
                project(i)
            attention_dve(dve, link, split_lo)
            for n in range(KC):
                operand_lo("attn", n, a_hi, a_lo, qT[:, n, :])

            def add_product(u, j, n):
                dve.wait_ge(product, n_product[u, j])
                xn = halves(xT[:, n, :])
                dve.tensor_tensor(xn, bank2(j, T // 2), xn, ALU.add).then_inc(free_dve, 1)

            for i in range(4):
                split_lo(FIRST["attn_out"] + i + 1)
                for j in range(2):
                    add_product(FIRST["attn_out"] + i, j, 2 * i + j)
            for n in range(KC):
                operand_lo("ffn0", n, a_hi, a_lo, xT[:, n, :], 1)
            for l in range(2):
                if l:
                    for i in range(4):
                        split_lo(FIRST["gmlp_v"] + i + 1)
                        if i == 0:
                            inverse_col("mix1")
                            inverse_row("mix1")
                    dve.wait_ge(v_rms, n_v_rms[0])
                    link(dve.reciprocal(rcol[:, 7, :], rcol[:, 6, :]))
                    dve.wait_ge(s_vgain, 16)
                    for t in range(TT):
                        dve.scalar_tensor_tensor(out=v_tok[:, t, :], in0=v_tok[:, t, :], scalar=rcol[:, 7, t:t + 1],
                                                 in1=vgain[:, :], op0=ALU.mult, op1=ALU.mult).then_inc(v_norm, 1)
                    for i in range(4):
                        u = FIRST["gmlp_u"] + i
                        split_lo(u + 1)
                        for j in range(2):
                            n = 2 * i + j
                            dve.wait_ge(product, n_product[u, j])
                            if n:
                                dve.wait_ge(op_lo, n_op_lo["gate", n - 1])
                            dve.tensor_tensor(halves(u_act[:, :]), bank2(j, T // 2), halves(inv_rms[:, :]), ALU.mult)\
                               .then_inc(free_dve, 1)
                            dve.wait_ge(mix_ready, n_mix_ready[n])
                            o = 2048 + 1024 * (n % 2)
                            tiles = "p (a t) -> p a t"
                            dve.tensor_tensor(mixed[:, 0:TP].rearrange(tiles, a=4), flat[:, o:o + TP].rearrange(tiles, a=4),
                                              sbias[n % 2][:, :].unsqueeze(1).broadcast_to([P, 4, P]), ALU.add)
                            dve.tensor_tensor(seqs(mixed[:, TP:T]), seqs(flat[:, o + TP:o + T]),
                                              sbias[n % 2][:, 0:TQ].unsqueeze(1).broadcast_to([P, NB, TQ]), ALU.add)\
                               .then_inc(mix_taken, 1)
                            dve.wait_ge(mix_taken, n_mix_taken[n])
                            dve.wait_ge(u_gelu, n_u_gelu[n])
                            dve.tensor_tensor(u_act[:, :], u_act[:, :], mixed[:, :], ALU.mult).then_inc(gated, 1)
                            operand_lo("gate", n, a_hi, a_lo, u_act[:, :])
                    for i in range(4):
                        split_lo(FIRST["gmlp_out"] + i + 1)
                        for j in range(2):
                            add_product(FIRST["gmlp_out"] + i, j, 2 * i + j)
                    for n in range(KC):
                        operand_lo("ffn1", n, a_hi, a_lo, xT[:, n, :], 4)
                for q, np_ in enumerate(PARTS):
                    for i in range(np_):
                        c = off_part[q] + i
                        u = FIRST[f"up{l}{q}"] + i
                        split_lo(u + 1)
                        if q == i == 0:
                            inverse_row(f"ffn{l}")
                        ci, co = conv_in[c % 2], conv[c % 2]
                        if c >= 2:
                            dve.wait_ge(tail, n_tail[l, c - 2])
                        dve.wait_ge(pads, n_pads[l, c])
                        for j in range(2):
                            dve.wait_ge(product, n_product[u, j])
                            dve.tensor_tensor(halves(ci[j][:, 2:2 + TP]), bank2(j, 256), halves(inv_rms[:, 0:TP]), ALU.mult)
                            dve.tensor_tensor(padded18(ci[j]), seqs(psum[:, 2 * j + 1, 256:384]), seqs(inv_rms[:, TP:T]),
                                              ALU.mult).then_inc(free_dve, 1)
                        for j in range(2):
                            dve.wait_ge(conv0, n_conv0[l, c, j])
                            ch = j * FC + c
                            link(dve.scalar_tensor_tensor(out=co[j][:, :], in0=ci[j][:, 1:1 + CW], scalar=convw[:, l, ch, 1:2],
                                                          in1=co[j][:, :], op0=ALU.mult, op1=ALU.add))
                            dve.scalar_tensor_tensor(out=co[j][:, :], in0=ci[j][:, 0:CW], scalar=convw[:, l, ch, 0:1],
                                                     in1=co[j][:, :], op0=ALU.mult, op1=ALU.add).then_inc(conv_done, 1)
                        dve.wait_ge(silu_done, n_silu_done[l, c])
                        dve.wait_ge(conv_done, n_conv_done[l, c, 1])
                        if c:
                            dve.wait_ge(h_lo, n_h_lo[l, c - 1])
                        dve.tensor_tensor(hidden[:, 0:TP], silu[:, 0:TP], co[1][:, 0:TP], ALU.mult)
                        dve.tensor_tensor(seqs(hidden[:, TP:T]), padded16(silu), padded16(co[1]), ALU.mult)\
                           .then_inc(h_ready, 1)
                        dve.wait_ge(h_hi, n_h_hi[l, c])
                        dve.tensor_tensor(g_lo[:, i, :], hidden[:, :], f32(g_hi[:, i, :]), ALU.subtract).then_inc(h_lo, 1)
                    for i in range(4):
                        u = FIRST[f"down{l}{q}"] + i
                        split_lo(u + 1)
                        final = q == len(PARTS) - 1
                        for j in range(2):
                            add_product(u, j, 2 * i + j)
                        if final:
                            for n in (2 * i, 2 * i + 1):
                                operand_lo(f"ple{l}", n, a_hi, a_lo, xT[:, n, :], 2 if l == 0 else 5)
                dve.wait_ge(p_hi_ready, n_p_hi_ready[l])
                dve.tensor_tensor(p_lo[:, :, :], p_raw[:, :, :], f32(p_hi[:, :, :]), ALU.subtract).then_inc(p_lo_ready, 1)
                for i in range(4):
                    u = FIRST[f"ple{l}"] + 2 * i + 1
                    split_lo(u)
                    if i == 0:
                        inverse_row(f"ple{l}")
                    split_lo(u + 1)
                    for j in range(2):
                        dve.wait_ge(product, n_product[u, j])
                        dve.tensor_tensor(halves(gate[:, j, :]), bank2(j, T // 2), halves(inv_rms[:, :]), ALU.mult)\
                           .then_inc(free_dve, 1)
                    for j in range(2):
                        n = 2 * i + j
                        dve.wait_ge(gate_done, n_gate_done[l, n])
                        dve.wait_ge(proj_ready, n_proj_ready[l, n])
                        link(dve.tensor_tensor(gate[:, j, :], gate[:, j, :], proj[:, j, :], ALU.mult))
                        dve.tensor_tensor(xT[:, n, :], xT[:, n, :], gate[:, j, :], ALU.add).then_inc(x_ready, 1)
                    if l == 0:
                        for n in (2 * i, 2 * i + 1):
                            operand_lo("mix1", n, g_hi, g_lo, xT[:, n, :], 3)

        def keep_tail(pool, l, c):
            if l and c == 0:
                pool.wait_ge(s_tails, 16)
            for j in range(2):
                pool.wait_ge(free_dve, n_free_dve[up_unit[l, c], j])
                ins = pool.tensor_copy(tails[:, j * FC + c, :].rearrange("p (i e) -> p i e", e=2),
                                       padded(conv_in[c % 2][j], NB + 1))
            ins.then_inc(tail, 1)

        def gated_mlp_pool(pool):
            for n in range(KC):
                pool.wait_ge(s_spat[n % 2], 48 * (n // 2 + 1))
                pool.affine_select(out=spat[n % 2][:, :, :], in_=spat[n % 2][:, :, :], compare_op=ALU.is_ge, fill=0.0,
                                   base=0, pattern=[[0, 2], [1, P]], channel_multiplier=-1).then_inc(tril, 1)
                if n == 0:
                    pool.wait_ge(v_norm, len(n_v_norm))
                    pool.dma_start(gv_out, v_tok[:, TT - 1, :]).then_inc(s_gv, 16)


        @block.gpsimd
        def _(pool):
            pool.memset(ones[:, :], 1.0).then_inc(s_const_pool, 1)
            pool.memset(eps[:, :], EPS).then_inc(s_const_pool, 1)
            pool.memset(qi_blk[:, :, :], 0.0).then_inc(s_const_pool, 1)

            def add_squares(norm):
                for n in range(KC):
                    k = norm_keys.index((norm, n))
                    pool.wait_ge(squared, n_squared[norm_keys[k]])
                    if k:
                        pool.wait_ge(summed, n_summed[norm_keys[k - 1]])
                    if n == 0:
                        i = NORMS.index(norm)
                        if i:
                            if i > 1:
                                pool.wait_ge(row_sum, n_row_sum[NORMS[i - 1]])
                            if i in (1, 4):
                                pool.wait_ge(col_sum, n_col_sum[NORMS[i - 1]])
                        ins = pool.tensor_copy(square_sum[:, :], square[:, k % 2, :])
                    else:
                        ins = pool.tensor_tensor(square_sum[:, :], square_sum[:, :], square[:, k % 2, :], ALU.add)
                    ins.then_inc(summed, 1)

            add_squares("mix0")
            pool.wait_ge(z_done, n_z_done[4])
            cols = "p t (g d) -> p t g d"
            pool.dma_start(k_out[0:TP].rearrange("(t p) c -> p t c", p=P), z[0][:, 0:4, :]).then_inc(s_kvout, 16)
            pool.dma_start(k_out[TP:T], z[0][:, 4, :]).then_inc(s_kvout, 16)
            pool.wait_ge(free_act, n_free_act[5, 1])
            pool.dma_start(v_out[0:TP].rearrange("(t p) c -> p t c", p=P), vtok[:, 0:4, :]).then_inc(s_kvout, 16)
            pool.dma_start(v_out[TP:T], vtok[:, 4, :]).then_inc(s_kvout, 16)
            pool.wait_ge(z_done, n_z_done[8])
            pool.dma_start(ki_out[0:TP].rearrange("(t p) c -> p t c", p=P), z[0][:, 0:4, 0:DI]).then_inc(s_kiout, 16)
            pool.dma_start(ki_out[TP:T], z[0][:, 4, 0:DI]).then_inc(s_kiout, 16)
            after_projection(pool)
            pool.memset(w_sel[:, :], 0.0).then_inc(pool_zero, 1)
            for b in range(NB):
                if b >= 2:
                    pool.wait_ge(idx_ready, n_idx_ready[n_pi + 3 * (b - 2) + 2])
                pool.tensor_copy(kidx_b[b % 2][:, PAST:KEYS], kiT[:, TP + TQ * b:TP + TQ * b + TQ]).then_inc(kidx_new, 1)
            pool.wait_ge(idx_ready, len(n_idx_ready))
            for b in range(NB):
                if b >= 2:
                    pool.wait_ge(logits, n_logits[NPA + b - 2])
                pool.tensor_copy(key_b[b % 2][:, :, PAST:KEYS], kT[:, :, TP + TQ * b:TP + TQ * b + TQ]).then_inc(key_new, 1)
            add_squares("ffn0")
            for l in range(2):
                if l:
                    gated_mlp_pool(pool)
                    add_squares("ffn1")
                pool.wait_ge(free_dve, n_free_dve[FIRST["gmlp_out" if l else "attn_out"], 0])
                if l:
                    pool.wait_ge(s_gv, 16)
                for ci in conv_in:
                    for c in ci:
                        last = pool.memset(c[:, 0:2], 0.0)
                pool.wait_ge(s_past, 16 * (l + 1))
                for c in range(FC):
                    if c >= 2:
                        pool.wait_ge(conv_done, n_conv_done[l, c - 2, 1])
                    for j in range(2):
                        ch = j * FC + c
                        ins = pool.tensor_copy(conv_in[c % 2][j][:, TP + 2:TP + 2 + NB * (TQ + 2)]
                                               .rearrange("p (b e) -> p b e", e=TQ + 2)[:, :, 0:2],
                                               pastT[:, ch, :].rearrange("p (b e) -> p b e", e=2))
                    ins.then_inc(pads, 1)
                    if c >= 1:
                        keep_tail(pool, l, c - 1)
                keep_tail(pool, l, FC - 1)
                pool.wait_ge(tail, n_tail[l, FC - 1])
                pool.dma_start(conv_out[:, l], tails[:, :, :]).then_inc(s_tails, 16)
                add_squares(f"ple{l}")
                if l == 0:
                    add_squares("mix1")
            for n in range(KC):
                pool.wait_ge(x_ready, n_x_ready["out", n])
                pool.dma_start(yT_out[:, n, :], xT[:, n, :]).then_inc(s_y, 16)
            pool.wait_ge(s_y, 16 * KC)
            pool.wait_ge(s_tails, 32)
            pool.wait_ge(s_gv, 16)
            pool.wait_ge(s_kvout, 64)
            pool.wait_ge(s_kiout, 32)

def kernel(**inputs):
    import numpy as np
    import concourse.bacc as _bacc
    from concourse import mybir as _mybir
    from concourse.bass_utils import run_bass_kernel_spmd as _run
    import ml_dtypes

    a = {k: np.asarray(v) for k, v in inputs.items()}

    def unit(w, rows, cols):
        r0, r1 = rows
        return np.concatenate([w[r0:r1, c0:c1] for c0, c1 in cols], axis=1)\
            .reshape((r1 - r0) // P, P, -1).transpose(1, 0, 2).reshape(-1)

    off = [sum(PARTS[:q]) for q in range(len(PARTS))]
    parts = []
    for name, i, k in UNITS:
        if name == "qkv":
            parts.append(unit(a["attn_w_in"][0], (0, D), [(WU * i, min(WU * i + WU, ZEND))]))
        elif name == "attn_out":
            parts.append(unit(a["attn_w_out"][0], (0, D), [(WU * i, WU * i + WU)]))
        elif name == "gmlp_v":
            parts.append(unit(a["gmlp_w_in"][0], (0, D), [(D + WU * i, D + WU * i + WU)]))
        elif name == "gmlp_u":
            parts.append(unit(a["gmlp_w_in"][0], (0, D), [(WU * i, WU * i + WU)]))
        elif name == "gmlp_out":
            parts.append(unit(a["gmlp_w_out"][0], (0, D), [(WU * i, WU * i + WU)]))
        elif name[:2] == "up":
            c = P * (off[int(name[3])] + i)
            parts.append(unit(a["ffn_w_up"][int(name[2])], (0, D), [(c, c + P), (FF + c, FF + c + P)]))
        elif name[:4] == "down":
            r = P * off[int(name[5])]
            parts.append(unit(a["ffn_w_down"][int(name[4])], (r, r + P * k), [(WU * i, WU * i + WU)]))
        else:
            w, c = a["ple_w_proj" if k == PC else "ple_w_gate"][int(name[3])], WU * (i // 2)
            parts.append(unit(w, (0, P * k), [(c, c + WU)]))
    weights = np.concatenate(parts)

    def chunked(rows):
        return np.ascontiguousarray(rows.T.reshape(-1, P, rows.shape[0]).transpose(1, 0, 2))

    def both(p, s):
        return np.concatenate([p.reshape(-1, p.shape[-1]), s.reshape(-1, s.shape[-1])])

    pos = np.concatenate([np.arange(TP), PAST + np.arange(TS) % TQ]).astype(np.float32)
    tables = []
    for half, r in ((16, 32), (8, 16)):
        e = -np.arange(half, dtype=np.float32) * np.float32(2.0 / r)
        ang = (pos[:, None] * np.power(500000.0, e.astype(np.float64)).astype(np.float32)[None]).astype(np.float64)
        tables += [np.cos(ang), np.sin(ang)]
    rope = np.concatenate(tables, axis=1).astype(np.float32).reshape(TT, P, 48).transpose(1, 0, 2)
    row = np.arange(P)
    onehot = np.zeros((P, NB, P), np.float32)
    for b in range(NB):
        onehot[:, b] = (row[:, None] // TQ == b) & (row[:, None] % TQ == row[None] % TQ)
    qeq = (row[:, None] % TQ == np.arange(TQ)[None]).astype(np.float32)
    gains = np.stack([a["norm_mix"][0], a["norm_ffn"][0], a["norm_ple"][0],
                      a["norm_mix"][1], a["norm_ffn"][1], a["norm_ple"][1]])
    spat = a["gmlp_w_spatial"][0].transpose(2, 0, 1)
    spat_s = np.zeros((P, KC, P), np.float32)
    for b in range(NB):
        spat_s[TQ * b:TQ * b + TQ, :, TQ * b:TQ * b + TQ] = spat[:TQ, :, :TQ]
    convw = np.stack([np.concatenate([a["ffn_conv_w"][l], a["ffn_conv_b"][l][None]]).T.reshape(2 * FC, P, 4)
                      .transpose(1, 0, 2) for l in range(2)], axis=1)
    kidx = a["cache_kidx"][0].transpose(0, 2, 1)
    data = {
        "weights": weights,
        "xT": chunked(both(a["x_prompt"], a["x_sample"])),
        "pT": np.stack([chunked(both(a["p_prompt"][l], a["p_sample"][l])) for l in range(2)], axis=1),
        "gains": gains.reshape(6, KC, P).transpose(2, 0, 1),
        "qkgain": np.broadcast_to(np.stack([a["attn_q_norm"][0], a["attn_k_norm"][0]])[None], (P, 2, P)),
        "rope": rope,
        "ident": np.eye(P, dtype=np.float32),
        "onehot": onehot.reshape(P, NB * P).astype(ml_dtypes.bfloat16),
        "qeq": qeq,
        "keyT": a["cache_k"][0].transpose(0, 3, 2, 1),
        "val": a["cache_v"][0].reshape(NB, 8, P, G * P).transpose(0, 2, 1, 3),
        "kidxT": np.concatenate([kidx, kidx], axis=1),
        "pastT": np.stack([a["state_ffn_conv"][l].reshape(2 * NB, 2 * FC, P).transpose(2, 1, 0) for l in range(2)], axis=1),
        "convw": convw,
        "vgain": np.broadcast_to(a["gmlp_v_norm"][0][None], (P, D)),
        "spat": spat,
        "spat_s": spat_s,
        "sbias": np.broadcast_to(a["gmlp_b_spatial"][0][None], (P, KC, P)),
    }
    outs = {"yT": (P, KC, T), "k": (T, G * P), "v": (T, G * P), "ki": (T, DI), "gv": (TS, D),
            "conv": (P, 2, 2 * FC, 2 * (NB + 1))}
    nc = _bacc.Bacc("TRN2", target_bir_lowering=False, num_devices=1)
    arrays, args = {}, []
    for name, x in data.items():
        if name == "keyT":
            x = x.transpose(0, 1, 2, 3)
        x = np.ascontiguousarray(x)
        arrays[f"in_{name}"] = x
        args.append(nc.dram_tensor(f"in_{name}", x.shape, _mybir.dt.from_np(x.dtype), kind="ExternalInput").ap())
    for name, shape in outs.items():
        args.append(nc.dram_tensor(f"out_{name}", shape, F32, kind="ExternalOutput").ap())
    bass_hybrid_step(nc, *args)
    r = _run(nc, [arrays], core_ids=[0])
    o = {name: r.results[0][f"out_{name}"] for name in outs}
    y = o["yT"].transpose(2, 1, 0).reshape(T, D)
    tails = o["conv"].transpose(1, 3, 2, 0).reshape(2, NB + 1, 2, 2 * FF)
    return (y[:TP].reshape(1, TP, D), y[TP:].reshape(NB, TQ, D),
            o["k"][:TP].reshape(1, 1, TP, G, P), o["v"][:TP].reshape(1, 1, TP, G, P), o["ki"][:TP].reshape(1, 1, TP, DI),
            o["k"][TP:].reshape(1, NB, TQ, G, P), o["v"][TP:].reshape(1, NB, TQ, G, P), o["ki"][TP:].reshape(1, NB, TQ, DI),
            o["gv"].reshape(1, NB, TQ, D), tails[:, :1], tails[:, 1:])
```
